# Optimizing a Trainium2 kernel written in Bass

```python
import jax, jax.numpy as jnp
from jax import lax
import numpy as np

D_MODEL = 2048
BATCH = 1
SEQ = 256
DEPTH = 1

GRID_W = 64
CTX_LEN = 256
D_FF = 5632
N_MOD = 9
RET_HEADS = 8
RET_DK = 64
RET_DV = 128
RET_CHUNK = 128
RET_ROPE_BASE = 10000.0
MLA_HEADS = 8
MLA_Q_RANK = 512
MLA_KV_RANK = 256
MLA_NOPE = 128
MLA_ROPE = 64
MLA_V = 128
AXIAL_BASE = 10000.0
Q_BLOCK = 128
RMS_EPS = 1e-6
GN_EPS = 1e-5
MIX_OUT = RET_HEADS * RET_DV + MLA_HEADS * MLA_V
SPLITS = (RET_HEADS * RET_DK, RET_HEADS * RET_DK, RET_HEADS * RET_DV, RET_HEADS * RET_DV,
          MLA_Q_RANK, MLA_KV_RANK, MLA_ROPE)
MIX_IN = sum(SPLITS)

kernel_name = "hymba_retention_mla_macaron_dit"

def rms_norm(x, g):
    xf = x.astype(jnp.float32)
    y = xf * lax.rsqrt(jnp.mean(xf * xf, axis=-1, keepdims=True) + RMS_EPS)
    return (y * g.astype(jnp.float32)).astype(x.dtype)

def modulate(h, shift, scale):
    return h * (1.0 + scale) + shift

def swiglu(h, w_in, w_out):
    g, u = jnp.split(h @ w_in, 2, axis=-1)
    return (jax.nn.silu(g) * u) @ w_out

def rope_tables(pos, dim, base):
    inv = base ** (-jnp.arange(0, dim, 2, dtype=jnp.float32) / dim)
    ang = pos.astype(jnp.float32)[:, None] * inv[None, :]
    return jnp.cos(ang)[:, None, :], jnp.sin(ang)[:, None, :]

def rotate(x, cos, sin):
    x1, x2 = jnp.split(x, 2, axis=-1)
    return jnp.concatenate([x1 * cos - x2 * sin, x2 * cos + x1 * sin], axis=-1).astype(x.dtype)

def axial_rope(x, row_tab, col_tab):
    xr, xc = jnp.split(x, 2, axis=-1)
    return jnp.concatenate([rotate(xr, *row_tab), rotate(xc, *col_tab)], axis=-1)

def project(h, w_in, q_norm_g, w_uq, kv_norm_g, w_ukv):
    b, n, _ = h.shape
    idx = [int(i) for i in np.cumsum(SPLITS)[:-1]]
    rq, rk, rv, rg, cq, ckv, kr = jnp.split(h @ w_in, idx, axis=-1)
    rq = rq.reshape(b, n, RET_HEADS, RET_DK)
    rk = rk.reshape(b, n, RET_HEADS, RET_DK) * (RET_DK ** -0.5)
    rv = rv.reshape(b, n, RET_HEADS, RET_DV)
    q = (rms_norm(cq, q_norm_g) @ w_uq).reshape(b, n, MLA_HEADS, MLA_NOPE + MLA_ROPE)
    kv = (rms_norm(ckv, kv_norm_g) @ w_ukv).reshape(b, n, MLA_HEADS, MLA_NOPE + MLA_V)
    q_nope, q_rope = q[..., :MLA_NOPE], q[..., MLA_NOPE:]
    k_nope, v = kv[..., :MLA_NOPE], kv[..., MLA_NOPE:]
    k_rope = kr[:, :, None, :]
    return rq, rk, rv, rg, q_nope, q_rope, k_nope, k_rope, v

def mla_keys(k_nope, k_rope):
    k_rope = jnp.broadcast_to(k_rope, k_nope.shape[:-1] + (MLA_ROPE,))
    return jnp.concatenate([k_nope, k_rope], axis=-1)

def block_attention(q, k, v):
    b, nq, h, dq = q.shape
    nb = nq // Q_BLOCK
    scale = dq ** -0.5
    qb = jnp.moveaxis(q.reshape(b, nb, Q_BLOCK, h, dq), 1, 0)

    def one(qi):
        s = jnp.einsum('bqhd,bkhd->bhqk', qi, k).astype(jnp.float32) * scale
        p = jax.nn.softmax(s, axis=-1)
        return jnp.einsum('bhqk,bkhe->bqhe', p.astype(v.dtype), v)

    out = lax.map(one, qb)
    return jnp.moveaxis(out, 0, 1).reshape(b, nq, h * v.shape[-1])

def retention_chunked(q, k, v, log_gamma, s0, strict):
    b, h, n, dk = q.shape
    dv = v.shape[-1]
    cs = RET_CHUNK
    nc = n // cs
    qc = q.reshape(b, h, nc, cs, dk)
    kc = k.reshape(b, h, nc, cs, dk)
    vc = v.reshape(b, h, nc, cs, dv)
    idx = jnp.arange(cs, dtype=jnp.float32)
    diff = idx[:, None] - idx[None, :]
    mask = diff > 0 if strict else diff >= 0
    lg = log_gamma[:, None, None]
    dmat = jnp.where(mask[None], jnp.exp(lg * jnp.where(mask, diff, 0.0)[None]), 0.0)
    scores = jnp.einsum('bhnid,bhnjd->bhnij', qc, kc) * dmat[None, :, None]
    y_inner = jnp.einsum('bhnij,bhnje->bhnie', scores, vc)
    zeta = jnp.exp(log_gamma[:, None] * (cs - 1 - idx)[None, :])
    xi = jnp.exp(log_gamma[:, None] * (idx + 1.0)[None, :])
    kv = jnp.einsum('bhnjd,bhnje->bhnde', kc * zeta[None, :, None, :, None], vc)
    decay_chunk = jnp.exp(log_gamma * cs)[None, :, None, None]

    def step(s, kv_n):
        return decay_chunk * s + kv_n, s

    s_final, s_prev = lax.scan(step, s0, jnp.moveaxis(kv, 2, 0))
    s_prev = jnp.moveaxis(s_prev, 0, 2)
    y_cross = jnp.einsum('bhnid,bhnde->bhnie', qc * xi[None, :, None, :, None], s_prev)
    return (y_inner + y_cross).reshape(b, h, n, dv), s_final

def bidir_retention(q, k, v, lg_f, lg_b, s0_f, s0_b):
    y_f, s_f = retention_chunked(q, k, v, lg_f, s0_f, False)
    y_b, s_b = retention_chunked(jnp.flip(q, 2), jnp.flip(k, 2), jnp.flip(v, 2), lg_b, s0_b, True)
    return y_f + jnp.flip(y_b, 2), s_f, s_b

def retention_output(y, gate):
    mu = jnp.mean(y, axis=-1, keepdims=True)
    var = jnp.mean(jnp.square(y - mu), axis=-1, keepdims=True)
    y = (y - mu) * lax.rsqrt(var + GN_EPS)
    b, h, n, dv = y.shape
    y = jnp.swapaxes(y, 1, 2).reshape(b, n, h * dv)
    return (jax.nn.silu(gate.astype(jnp.float32)) * y).astype(gate.dtype)

def setup_inputs(seed: int = 0) -> dict:
    key = jax.random.key(seed)
    ks = jax.random.split(key, 24)
    f32 = jnp.float32

    def nrm(k, shape, scale):
        return jax.random.normal(k, shape, f32) * scale

    gam = 1.0 - 2.0 ** (-5.0 - jnp.arange(RET_HEADS, dtype=f32))
    decay_logit = jnp.log(gam) - jnp.log1p(-gam)
    return {
        "x": nrm(ks[0], (BATCH, SEQ, D_MODEL), 1.0),
        "c": nrm(ks[1], (BATCH, D_MODEL), 1.0),
        "ctx": nrm(ks[2], (BATCH, CTX_LEN, D_MODEL), 1.0),
        "c_ctx": nrm(ks[3], (D_MODEL,), 1.0),
        "ada_w": nrm(ks[4], (DEPTH, D_MODEL, N_MOD * D_MODEL), 0.5 * D_MODEL ** -0.5),
        "ada_b": nrm(ks[5], (DEPTH, N_MOD * D_MODEL), 0.02),
        "norm1_g": 1.0 + nrm(ks[6], (DEPTH, D_MODEL), 0.02),
        "ffn1_w_in": nrm(ks[7], (DEPTH, D_MODEL, 2 * D_FF), D_MODEL ** -0.5),
        "ffn1_w_out": nrm(ks[8], (DEPTH, D_FF, D_MODEL), D_FF ** -0.5),
        "norm2_g": 1.0 + nrm(ks[9], (DEPTH, D_MODEL), 0.02),
        "mix_w_in": nrm(ks[10], (DEPTH, D_MODEL, MIX_IN), D_MODEL ** -0.5),
        "ret_decay_fwd": decay_logit[None, :] + nrm(ks[11], (DEPTH, RET_HEADS), 0.05),
        "ret_decay_bwd": decay_logit[None, :] + nrm(ks[12], (DEPTH, RET_HEADS), 0.05),
        "mla_q_norm_g": 1.0 + nrm(ks[13], (DEPTH, MLA_Q_RANK), 0.02),
        "mla_w_uq": nrm(ks[14], (DEPTH, MLA_Q_RANK, MLA_HEADS * (MLA_NOPE + MLA_ROPE)), MLA_Q_RANK ** -0.5),
        "mla_kv_norm_g": 1.0 + nrm(ks[15], (DEPTH, MLA_KV_RANK), 0.02),
        "mla_w_ukv": nrm(ks[16], (DEPTH, MLA_KV_RANK, MLA_HEADS * (MLA_NOPE + MLA_V)), MLA_KV_RANK ** -0.5),
        "mix_w_out": nrm(ks[17], (DEPTH, MIX_OUT, D_MODEL), MIX_OUT ** -0.5),
        "norm3_g": 1.0 + nrm(ks[18], (DEPTH, D_MODEL), 0.02),
        "ffn2_w_in": nrm(ks[19], (DEPTH, D_MODEL, 2 * D_FF), D_MODEL ** -0.5),
        "ffn2_w_out": nrm(ks[20], (DEPTH, D_FF, D_MODEL), D_FF ** -0.5),
        "final_norm_g": 1.0 + nrm(ks[21], (D_MODEL,), 0.02),
    }

def reference(x, c, ctx, c_ctx, ada_w, ada_b, norm1_g, ffn1_w_in, ffn1_w_out, norm2_g,
              mix_w_in, ret_decay_fwd, ret_decay_bwd, mla_q_norm_g, mla_w_uq, mla_kv_norm_g,
              mla_w_ukv, mix_w_out, norm3_g, ffn2_w_in, ffn2_w_out, final_norm_g):
    b, n_lat, d = x.shape
    n_rows = n_lat // GRID_W
    pos_row = jnp.repeat(jnp.arange(n_rows), GRID_W)
    pos_col = jnp.tile(jnp.arange(GRID_W), n_rows)
    row_tab = rope_tables(pos_row, MLA_ROPE // 2, AXIAL_BASE)
    col_tab = rope_tables(pos_col, MLA_ROPE // 2, AXIAL_BASE)
    ret_tab = rope_tables(jnp.arange(n_lat), RET_DK, RET_ROPE_BASE)
    s_zero = jnp.zeros((b, RET_HEADS, RET_DK, RET_DV), jnp.float32)

    def heads(t):
        return jnp.swapaxes(t, 1, 2).astype(jnp.float32)

    for l in range(DEPTH):
        is_last = l == DEPTH - 1
        m_lat = (jax.nn.silu(c) @ ada_w[l] + ada_b[l]).reshape(b, N_MOD, 1, d)
        m_ctx = (jax.nn.silu(c_ctx)[None, :] @ ada_w[l] + ada_b[l]).reshape(1, N_MOD, 1, d)

        x = x + 0.5 * m_lat[:, 2] * swiglu(modulate(rms_norm(x, norm1_g[l]), m_lat[:, 0], m_lat[:, 1]),
                                           ffn1_w_in[l], ffn1_w_out[l])
        ctx = ctx + 0.5 * m_ctx[:, 2] * swiglu(modulate(rms_norm(ctx, norm1_g[l]), m_ctx[:, 0], m_ctx[:, 1]),
                                               ffn1_w_in[l], ffn1_w_out[l])

        hx = modulate(rms_norm(x, norm2_g[l]), m_lat[:, 3], m_lat[:, 4])
        hc = modulate(rms_norm(ctx, norm2_g[l]), m_ctx[:, 3], m_ctx[:, 4])
        rq, rk, rv, rg, qn, qr, kn, kr, v = project(
            hx, mix_w_in[l], mla_q_norm_g[l], mla_w_uq[l], mla_kv_norm_g[l], mla_w_ukv[l])
        crq, crk, crv, crg, cqn, cqr, ckn, ckr, cv = project(
            hc, mix_w_in[l], mla_q_norm_g[l], mla_w_uq[l], mla_kv_norm_g[l], mla_w_ukv[l])

        lg_f = jax.nn.log_sigmoid(ret_decay_fwd[l].astype(jnp.float32))
        lg_b = jax.nn.log_sigmoid(ret_decay_bwd[l].astype(jnp.float32))
        y_ctx, s_f, s_b = bidir_retention(heads(crq), heads(crk), heads(crv), lg_f, lg_b, s_zero, s_zero)
        rq = rotate(rq, *ret_tab)
        rk = rotate(rk, *ret_tab)
        y_lat, _, _ = bidir_retention(heads(rq), heads(rk), heads(rv), lg_f, lg_b, s_f, s_b)
        ret_out = retention_output(y_lat, rg)

        q_lat = jnp.concatenate([qn, axial_rope(qr, row_tab, col_tab)], axis=-1)
        k_lat = mla_keys(kn, axial_rope(kr, row_tab, col_tab))
        k_ctx = mla_keys(ckn, ckr)
        k_all = jnp.concatenate([k_lat, k_ctx], axis=1)
        v_all = jnp.concatenate([v, cv], axis=1)
        mla_out = block_attention(q_lat, k_all, v_all)

        mix = jnp.concatenate([ret_out.astype(x.dtype), mla_out.astype(x.dtype)], axis=-1) @ mix_w_out[l]
        x = x + m_lat[:, 5] * mix
        if not is_last:
            ctx_ret = retention_output(y_ctx, crg)
            ctx_mla = block_attention(jnp.concatenate([cqn, cqr], axis=-1), k_ctx, cv)
            ctx_mix = jnp.concatenate([ctx_ret.astype(ctx.dtype), ctx_mla.astype(ctx.dtype)], axis=-1) @ mix_w_out[l]
            ctx = ctx + m_ctx[:, 5] * ctx_mix

        x = x + 0.5 * m_lat[:, 8] * swiglu(modulate(rms_norm(x, norm3_g[l]), m_lat[:, 6], m_lat[:, 7]),
                                           ffn2_w_in[l], ffn2_w_out[l])
        if not is_last:
            ctx = ctx + 0.5 * m_ctx[:, 8] * swiglu(modulate(rms_norm(ctx, norm3_g[l]), m_ctx[:, 6], m_ctx[:, 7]),
                                                   ffn2_w_in[l], ffn2_w_out[l])

    return rms_norm(x, final_norm_g)


_drawn_inputs = setup_inputs


def setup_inputs(seed=0):
    import zlib

    import numpy as np

    out = dict(_drawn_inputs(seed))
    spreads = {}
    factors = {'ada_b': 2.892,
     'norm1_g': 8.0,
     'norm2_g': 8.0,
     'mla_q_norm_g': 8.0,
     'mla_w_uq': 2.944,
     'mla_kv_norm_g': 8.0,
     'norm3_g': 23.654,
     'final_norm_g': 7.788}
    for name, (base, spread) in spreads.items():
        noise = np.random.default_rng([zlib.crc32(name.encode()), seed]).standard_normal(out[name].shape)
        drawn = base * np.exp(spread * noise) if base else spread * noise
        out[name] = __import__('jax').numpy.asarray(drawn.astype(out[name].dtype))
    for name, factor in factors.items():
        out[name] = (out[name] * factor).astype(out[name].dtype)
    return out
```

```python
import numpy as np
from concourse import mybir
import concourse.bass as bass


F32 = mybir.dt.float32
F32R = mybir.dt.float32r
ACT = mybir.ActivationFunctionType
ALU = mybir.AluOpType
AX = mybir.AxisListType
ds = bass.ds

P = 128
D = 2048
KT = D // P
LAT = 256
CTX = 256
TOK = LAT + CTX
DFF = 5632
HEADS = 8
DK = 64
ROPE = 64
GRID_W = 64
QT = 4
CT = 2
RMS_EPS = 1e-6
GN_EPS = 1e-5
MLA_SCALE = float(P + ROPE) ** -0.5

SLAB = 2048
RAW = 4
GROUP = 4
GROUPS = DFF // P // GROUP
GSLABS = 3 * GROUP
FSLABS = GROUPS * GSLABS
ADA_SLABS = 3 * KT
FFN1_0 = ADA_SLABS
MIX0 = FFN1_0 + FSLABS
S_RG, S_CQ, S_RQ, S_CKV, S_KR, S_RK, S_RV = 0, 8, 12, 16, 18, 19, 23
S_UQ, S_UKV, S_OUTR, S_OUTM, MSLABS = 31, 34, 36, 44, 52
FFN2_0 = MIX0 + MSLABS
SLABS = FFN2_0 + FSLABS
CH = 1024
C_RQ, C_RK, C_RV, C_RG, C_CQ, C_CKV, C_KR = 0, 512, 1024, 2048, 3072, 3584, 3840
V_N1, V_N2, V_N3, V_NF, V_C, V_CC, V_QG, V_KG, VROWS = 0, 16, 32, 48, 64, 80, 96, 100, 102
Y_F1 = KT
Y_OUT = Y_F1 + GROUPS * KT
Y_F2 = Y_OUT + KT


def constants():
    ident = np.eye(P, dtype=np.float32)
    p = np.arange(P)
    swap32 = ident[p ^ 32]
    swap16 = ident[p ^ 16]
    tok = np.arange(LAT, dtype=np.float32)

    def tables(inv, pos, half, swap):
        ang = (pos * inv[:, None]).astype(np.float32)
        sign = np.where((p & half) == 0, -1.0, 1.0).astype(np.float32)[:, None]
        return np.cos(ang).astype(np.float32), (np.sin(ang) * sign).astype(np.float32)

    inv = (np.float32(10000.0) ** (-(2.0 * (p % 32)).astype(np.float32) / np.float32(DK))).astype(np.float32)
    rc, rs = tables(inv, tok[None, :], 32, swap32)
    inv = (np.float32(10000.0) ** (-(2.0 * (p % 16)).astype(np.float32) / np.float32(ROPE // 2))).astype(np.float32)
    row, col = np.floor(tok / GRID_W), tok % GRID_W
    pos = np.where(((p % 64) < 32)[:, None], row[None, :], col[None, :]).astype(np.float32)
    ac, as_ = tables(inv, pos, 16, swap16)
    rope = np.concatenate([rc, rs, ac, as_], axis=1)
    dist = np.zeros((P, 2, 4, LAT), np.float32)
    for jt in range(2):
        j = (jt * P + p)[:, None].astype(np.float32)
        dist[:, 0, jt] = np.maximum(tok[None] - j, 0)
        dist[:, 1, jt] = np.maximum(j - tok[None], 0)
        dist[:, 0, 2 + jt] = CTX + tok[None] - j
        dist[:, 1, 2 + jt] = j + LAT - tok[None]
    return {"eye": np.concatenate([ident, swap32, swap16], axis=1), "rope": rope,
            "dist": dist.reshape(P, -1)}


def build(nc, x, c, ctx, c_ctx, ada_w, ada_b, norm1_g, ffn1_w_in, ffn1_w_out, norm2_g,
          mix_w_in, ret_decay_fwd, ret_decay_bwd, mla_q_norm_g, mla_w_uq, mla_kv_norm_g,
          mla_w_ukv, mix_w_out, norm3_g, ffn2_w_in, ffn2_w_out, final_norm_g,
          eye, rope, dist, out):
    base = (nc.sbuf_base + 31) // 32 * 32
    KB = 1024
    o_xl = base
    o_xc = o_xl + 16 * KB
    o_hh = o_xc + 16 * KB
    o_hl = o_hh + 32 * KB
    o_wh = o_hl + 32 * KB
    o_wl = o_wh + 16 * KB
    o_raw = o_wl + 16 * KB
    o_a = o_raw + 32 * KB
    o_e = o_a + 16 * KB
    o_m = o_e + 16 * KB

    def at(name, shape, dt, off):
        return nc.alloc_sbuf_tensor_at(name, shape, dt, offset=off)

    small = [o_m]

    def sm(name, shape, dt=F32):
        t = at(name, shape, dt, small[0])
        n = int(np.prod(shape[1:])) * 4
        small[0] += (n + 31) // 32 * 32
        return t

    xl = at("xl", [P, KT, LAT], F32, o_xl)
    xc = at("xc", [P, KT, CTX], F32, o_xc)
    hh = at("hh", [P, KT, TOK], F32R, o_hh)
    hl = at("hl", [P, KT, TOK], F32R, o_hl)
    wh = at("wh", [P, 2, SLAB], F32R, o_wh)
    wl = at("wl", [P, 2, SLAB], F32R, o_wl)
    raw = at("raw", [P, RAW, SLAB], F32, o_raw)
    ah = at("ah", [P, GROUP, TOK], F32R, o_a)
    al = at("al", [P, GROUP, TOK], F32R, o_a + 8 * KB)
    chunk = at("chunk", [P, 2, CH], F32, o_e)
    accl = at("accl", [P, CH], F32, o_e + 8 * KB)
    accc = at("accc", [P, CH], F32, o_e + 12 * KB)
    xnat = at("xnat", [P, 4, D], F32, o_hl)
    vnat = at("vnat", [VROWS, P], F32, o_a)
    bnat = at("bnat", [72, 2, P], F32, o_a + 1 * KB)
    csp = at("csp", [P, KT, P], F32R, o_a)
    hf = at("hf", [P, 2, TOK], F32, o_a + 8 * KB)
    xr = at("xr", [P, KT, TOK], F32, o_hl)
    rows = at("rows", [4, D], F32, o_e + 8 * KB)
    sq = at("sq", [P, 4, TOK], F32, o_e)
    ssum = at("ssum", [P, TOK], F32, o_e + 8 * KB)
    nt = at("nt", [P, 2, TOK], F32, o_e + 10 * KB)
    rq = at("rq", [P, 4, LAT], F32, o_a)
    cq = at("cq", [P, QT, LAT], F32, o_a + 4 * KB)
    rg = at("rg", [P, HEADS, LAT], F32, o_a + 8 * KB)
    rk = at("rk", [P, 4, TOK], F32, o_e)
    ckv = at("ckv", [P, CT, TOK], F32, o_e + 8 * KB)
    krope = at("krope", [P, TOK], F32, o_e + 12 * KB)
    rv = at("rv", [P, 4, HEADS * P], F32, o_xc)
    mixh = at("mixh", [P, 2 * HEADS, LAT], F32R, o_hh)
    mixl = at("mixl", [P, 2 * HEADS, LAT], F32R, o_hh + 16 * KB)
    yret = at("yret", [P, HEADS, LAT], F32, o_hh + 24 * KB)
    decay = at("decay", [P, 2, 4, LAT], F32, o_hl)
    pret = at("pret", [P, 2, 4, LAT], F32, o_hl + 8 * KB)
    far = at("far", [P, 2, 4, LAT], F32, o_hl + 16 * KB)
    dback = at("dback", [P, 2, 2, LAT], F32, o_hl + 24 * KB)
    lsq = at("lsq", [P, 1024], F32, o_hl + 28 * KB)
    ysq = at("ysq", [P, 2, 2 * LAT], F32, o_hl)
    ysd = at("ysd", [P, 2, 2 * LAT], F32, o_hl + 4 * KB)
    cqh = at("cqh", [P, QT, LAT], F32R, o_e)
    cql = at("cql", [P, QT, LAT], F32R, o_e + 4 * KB)
    ckvh = at("ckvh", [P, CT, TOK], F32R, o_hl + 20 * KB)
    ckvl = at("ckvl", [P, CT, TOK], F32R, o_hl + 24 * KB)
    qn = at("qn", [P, HEADS, LAT], F32, o_hl + 8 * KB)
    qr = at("qr", [P, HEADS // 2, LAT], F32, o_a)
    kn = at("kn", [P, HEADS, TOK], F32, o_xc)
    vm = [at("vm0", [P, 4, 4 * P], F32, o_a + 8 * KB), at("vm1", [P, 4, 4 * P], F32, o_hl)]
    pt = [at("pt0", [P, 4, LAT], F32, o_hl + 16 * KB), at("pt1", [P, 4, LAT], F32, o_e + 8 * KB)]
    pn = at("pn", [P, 2, TOK], F32, o_hl + 28 * KB)
    outn = at("outn", [P, 2, D], F32, o_hl)

    eyes = sm("eyes", [P, 3, P])
    ones = sm("ones", [P, P])
    sg = sm("sg", [P, TOK])
    ropes = at("ropes", [P, 4, LAT], F32, o_m + 4 * P * 4)
    act = sm("act", [P, TOK])
    rms = sm("rms", [P, TOK])
    rope_t = sm("rope_t", [P, LAT])
    vt = sm("vt", [P, VROWS])
    bt = sm("bt", [P, 9 * KT])
    cs = sm("cs", [P, KT, 2])
    ml = sm("ml", [P, 9 * KT])
    mc = sm("mc", [P, 5 * KT])
    a1l, a1c, a2l, a2c, a3l = (sm(n, [P, KT]) for n in ("a1l", "a1c", "a2l", "a2c", "a3l"))
    g1l, g1c, g3l = (sm(n, [P, KT]) for n in ("g1l", "g1c", "g3l"))
    eps = sm("eps", [P, 2])
    dummy = sm("dummy", [P, 1])
    dec = sm("dec", [P, 2 * HEADS])
    lg = sm("lg", [P, 2 * HEADS])
    lt = sm("lt", [P, 4, 2 * HEADS])
    mx = sm("mx", [P, 16])
    nm = sm("nm", [P, 16])
    rsum = sm("rsum", [P, 16])
    rrec = sm("rrec", [P, 16])
    red = sm("red", [P, 8])
    assert small[0] <= nc.sbuf_usable_end

    def bank(name):
        return nc.alloc_psum_tensor(name, [P, 512], F32)

    pg, pu, pa, pb = bank("pg"), bank("pu"), bank("pa"), bank("pb")
    py = [bank(f"py{i}") for i in range(4)]
    pgu = [pg, pu]
    pab = [pa, pb]

    sems = {}

    def sem(name):
        sems[name] = nc.alloc_semaphore(name)
        return sems[name]

    vec_loaded = sem("vec_loaded")
    x_loaded = sem("x_loaded")
    rope_loaded = sem("rope_loaded")
    far_loaded = sem("far_loaded")
    raw_loaded = [sem(f"raw_loaded{i}") for i in range(RAW)]
    wh_ready = sem("wh_ready")
    wl_ready = sem("wl_ready")
    slab_used = sem("slab_used")
    chunk_loaded = [sem("chunk_loaded0"), sem("chunk_loaded1")]
    chunk_free = sem("chunk_free")
    ada_summed = sem("ada_summed")
    vec_turned = sem("vec_turned")
    consts_ready = sem("consts_ready")
    vecs_ready = sem("vecs_ready")
    cs_ready = sem("cs_ready")
    pg_free, pu_free, pa_free = sem("pg_free"), sem("pu_free"), sem("pa_free")
    y_done, y_free = sem("y_done"), sem("y_free")
    x_turned, red_ready = sem("x_turned"), sem("red_ready")
    sq_ready, ss_added, ss_done = sem("sq_ready"), sem("ss_added"), sem("ss_done")
    csh_ready, csl_ready, rows_ready, rows_turned = sem("csh_ready"), sem("csl_ready"), sem("rows_ready"), sem("rows_turned")
    xr_ready, hf_ready, mods_ready = sem("xr_ready"), sem("hf_ready"), sem("mods_ready")
    rms_ready, nt_ready, hh_ready, hl_ready = sem("rms_ready"), sem("nt_ready"), sem("hh_ready"), sem("hl_ready")
    ah_ready, al_ready = sem("ah_ready"), sem("al_ready")
    proj_free = sem("proj_free")
    lsq_ready, lss_done, lrms_ready, lat_normed = sem("lsq_ready"), sem("lss_done"), sem("lrms_ready"), sem("lat_normed")
    cqh_ready, lat_split = sem("cqh_ready"), sem("lat_split")
    swapped, rope_done = sem("swapped"), sem("rope_done")
    lnu_ready = sem("lnu_ready")
    darg_ready, decay_ready = sem("darg_ready"), sem("decay_ready")
    rs_done, rp_ready, ry_done, ry_free = sem("rs_done"), sem("rp_ready"), sem("ry_done"), sem("ry_free")
    mu_done, yc_ready, ysq_ready, var_done = sem("mu_done"), sem("yc_ready"), sem("ysq_ready"), sem("var_done")
    ysd_ready, yn_ready, mixh_ready, mixl_ready = sem("ysd_ready"), sem("yn_ready"), sem("mixh_ready"), sem("mixl_ready")
    up_done, up_free = sem("up_done"), sem("up_free")
    sc_done, nm_ready, exp_done, pn_ready = sem("sc_done"), sem("nm_ready"), sem("exp_done"), sem("pn_ready")
    turned, pt_ready, o_done, oh_ready, ol_ready = sem("turned"), sem("pt_ready"), sem("o_done"), sem("oh_ready"), sem("ol_ready")
    fin_ready, out_ready, out_stored = sem("fin_ready"), sem("out_ready"), sem("out_stored")
    dve_chain, act_chain = sem("dve_chain"), sem("act_chain")

    def slab_at(t, m, a, b):
        return t[:, m % 2, a:b]

    ROOTS = (0, 2, 4, 5)
    TILES = (0, KT, 3 * KT)

    block = nc.Block()
    with block:

        @block.sync
        def _(sp):
            mw = mix_w_in[0].rearrange("(t p) n -> p t n", p=P)

            for row, v in ((V_N1, norm1_g[0]), (V_N2, norm2_g[0]), (V_N3, norm3_g[0]), (V_NF, final_norm_g),
                           (V_C, c[0]), (V_CC, c_ctx), (V_QG, mla_q_norm_g[0]), (V_KG, mla_kv_norm_g[0])):
                rows = v.rearrange("(t p) -> t p", p=P)
                sp.dma_start(vnat[row:row + rows.shape[0], :], rows).then_inc(vec_loaded, 16)
            sp.dma_start(bnat[:], ada_b[0].rearrange("(a q p) -> q a p", a=2, p=P)).then_inc(vec_loaded, 16)
            sp.dma_start(eyes[:].rearrange("p a b -> p (a b)"), eye).then_inc(vec_loaded, 16)

            def ada_slab(mod, t, slot):
                sp.dma_start(raw[:, slot, :], ada_w[0, t * P:(t + 1) * P, ds(mod * D, D)]).then_inc(raw_loaded[slot], 64)

            for t in range(RAW):
                ada_slab(0, t, t)
            for k in range(2):
                sp.dma_start(xnat[:, k, :], x[0, k * P:(k + 1) * P, :]).then_inc(x_loaded, 16)
                sp.dma_start(xnat[:, 2 + k, :], ctx[0, k * P:(k + 1) * P, :]).then_inc(x_loaded, 16)
            with sp.Fori(0, 2) as i:
                for t in range(RAW, RAW + KT):
                    sp.wait_ge(wl_ready, i * KT + (t - RAW + 1))
                    ada_slab(i + t // KT, t % KT, t % RAW)
            for t in range(RAW, KT):
                sp.wait_ge(wl_ready, 2 * KT + t - RAW + 1)
                ada_slab(2, t, t % RAW)

            def ffn_slab(w_in, w_out, group, s, slot):
                if s < 2 * GROUP:
                    col = group * (GROUP * P) + (s // 2) * P + (DFF if s % 2 else 0)
                    src = w_in[0].rearrange("(t p) n -> p t n", p=P)[:, :, ds(col, P)]
                    dst = raw[:, slot, :].rearrange("p (t n) -> p t n", n=P)
                else:
                    q = s - 2 * GROUP
                    src = w_out[0, ds(group * (GROUP * P), GROUP * P), q * 512:(q + 1) * 512].rearrange("(t p) n -> p t n", p=P)
                    dst = raw[:, slot, :].rearrange("p (t n) -> p t n", n=512)
                sp.dma_start(dst, src).then_inc(raw_loaded[slot], 64)

            def chunk_load(unit, t, count):
                sp.wait_ge(chunk_free, count + 1)
                sp.dma_start(chunk[:, t % 2, :], ada_w[0, t * P:(t + 1) * P, ds(unit * CH + 3 * D, CH)]).then_inc(chunk_loaded[t % 2], 16)

            for s in range(RAW):
                sp.wait_ge(wl_ready, FFN1_0 - RAW + s + 1)
                ffn_slab(ffn1_w_in, ffn1_w_out, 0, s, s)

            def ahead(i, s):
                sp.wait_ge(wl_ready, i * GSLABS + (FFN1_0 + s + 1))
                s4 = s + RAW
                ffn_slab(ffn1_w_in, ffn1_w_out, i + s4 // GSLABS, s4 % GSLABS, s4 % RAW)

            with sp.Fori(0, 4) as i:
                for s in range(GSLABS):
                    ahead(i, s)
                    if s < 8:
                        for t in (2 * s, 2 * s + 1):
                            chunk_load(i, t, i * KT + t)
            with sp.Fori(4, 8) as i:
                for s in range(GSLABS):
                    ahead(i, s)
                    if s < 4:
                        for t in range(4 * s, 4 * s + 4):
                            chunk_load(i * 2 - 4, t, (i - 4) * (2 * KT) + t + 4 * KT)
                    elif 5 <= s < 9:
                        for t in range(4 * s - 20, 4 * s - 16):
                            chunk_load(i * 2 - 3, t, (i - 4) * (2 * KT) + t + 5 * KT)
            for s in range(GSLABS - RAW):
                ahead(8, s)
            with sp.Fori(9, GROUPS) as i:
                for s in range(GSLABS):
                    sp.wait_ge(wl_ready, i * GSLABS + (FFN1_0 + s - RAW + 1))
                    ffn_slab(ffn1_w_in, ffn1_w_out, i, s, s % RAW)

            def mix_slab(s, src, dst=None, parts=1, first=True):
                m = MIX0 + s
                if first:
                    sp.wait_ge(wl_ready, m - RAW + 1)
                dst = raw[:, m % RAW, :] if dst is None else dst(raw[:, m % RAW, :])
                sp.dma_start(dst, src).then_inc(raw_loaded[m % RAW], 64 // parts)

            def tiles(n):
                return lambda r: r.rearrange("p (t n) -> p t n", n=n)

            def in_slabs(s, col, n):
                for j in range(n):
                    mix_slab(s + j, mw[:, :, col + j * P:col + (j + 1) * P], tiles(P))

            in_slabs(S_RG, C_RG, HEADS)
            in_slabs(S_CQ, C_CQ, QT)
            in_slabs(S_RQ, C_RQ, 4)
            in_slabs(S_CKV, C_CKV, CT)
            for half in range(2):
                mix_slab(S_KR, mw[:, :, C_KR:C_KR + ROPE],
                         lambda r: tiles(P)(r)[:, :, half * ROPE:(half + 1) * ROPE], 2, half == 0)
            in_slabs(S_RK, C_RK, 4)
            for half in range(2):
                for q in range(4):
                    mix_slab(S_RV + 4 * half + q, mw[:, 4 * q:4 * q + 4, C_RV + half * 512:C_RV + (half + 1) * 512], tiles(512))
            uq = mla_w_uq[0].rearrange("(t p) (h n) -> t p h n", p=P, n=P + ROPE)
            for half in range(2):
                for t in range(QT):
                    mix_slab(S_UQ + half, uq[t, :, 4 * half:4 * half + 4, 0:P],
                             lambda r: tiles(P)(r)[:, 4 * t:4 * t + 4, :], QT, t == 0)
            for t in range(QT):
                mix_slab(S_UQ + 2, uq[t, :, :, P:P + ROPE], lambda r: tiles(ROPE)(r)[:, 8 * t:8 * t + 8, :], QT, t == 0)
            ukv = mla_w_ukv[0].rearrange("(t p) (h n) -> t p h n", p=P, n=2 * P)
            for which in range(2):
                for t in range(CT):
                    mix_slab(S_UKV + which, ukv[t, :, :, which * P:(which + 1) * P],
                             lambda r: tiles(P)(r)[:, 8 * t:8 * t + 8, :], CT, t == 0)
            mo = mix_w_out[0].rearrange("(t p) n -> p t n", p=P)
            for part, s0 in ((0, S_OUTR), (HEADS, S_OUTM)):
                with sp.Fori(0, 2) as i:
                    for s in range(4):
                        sp.wait_ge(wl_ready, i * 4 + (MIX0 + s0 + s - RAW + 1))
                        sp.dma_start(tiles(LAT)(raw[:, (MIX0 + s0 + s) % RAW, :]),
                                     mo[:, part:part + HEADS, ds(i * 1024 + s * 256, 256)]).then_inc(raw_loaded[(MIX0 + s0 + s) % RAW], 64)
            with sp.Fori(0, GROUPS) as i:
                for s in range(GSLABS):
                    sp.wait_ge(wl_ready, i * GSLABS + (FFN2_0 + s - RAW + 1))
                    ffn_slab(ffn2_w_in, ffn2_w_out, i, s, s % RAW)

            for k in range(2):
                for q in range(4):
                    sp.wait_ge(out_ready, 2 * q + k + 1)
                    sp.dma_start(out[0, k * P:(k + 1) * P, q * 512:(q + 1) * 512], outn[:, k, q * 512:(q + 1) * 512]).then_inc(out_stored, 16)
            sp.wait_ge(out_stored, 8 * 16)

        @block.gpsimd
        def _(pool):
            nc.gpsimd.memset(ones[:], 1.0).then_inc(consts_ready, 1)
            nc.gpsimd.memset(eps[:, 0:1], RMS_EPS).then_inc(consts_ready, 1)
            nc.gpsimd.memset(eps[:, 1:2], GN_EPS).then_inc(consts_ready, 1)
            nc.gpsimd.memset(dummy[:], 0.0).then_inc(consts_ready, 1)
            pool.wait_ge(pg_free, 1)
            pool.wait_ge(pa_free, 1)
            nc.gpsimd.memset(csp[:].bitcast(F32).rearrange("p a b -> p (a b)"), 0.0).then_inc(consts_ready, 1)
            for f, w in enumerate((ret_decay_fwd, ret_decay_bwd)):
                pool.dma_start(dec[:, f * HEADS:(f + 1) * HEADS], w.to_broadcast([P, HEADS])).then_inc(rope_loaded, 16)
            pool.wait_ge(y_free, Y_OUT)
            pool.dma_start(ropes[:].rearrange("p a b -> p (a b)"), rope).then_inc(rope_loaded, 16)
            pool.wait_ge(slab_used, MIX0 + S_UQ)
            pool.dma_start(far[:].rearrange("p a b c -> p (a b c)"), dist).then_inc(far_loaded, 16)

        @block.scalar
        def _(se):
            count = [0]

            def link(ins):
                count[0] += 1
                ins.then_inc(act_chain, 1)
                se.wait_ge(act_chain, count[0])

            def split(m, slot, turn):
                se.wait_ge(raw_loaded[slot], turn * 64)
                if not (isinstance(m, int) and m < 2):
                    se.wait_ge(slab_used, m - 1)
                nc.scalar.activation(wh[:, slot % 2, :], raw[:, slot, :], ACT.Copy).then_inc(wh_ready, 1)

            def static_split(m):
                if m < SLABS:
                    split(m, m % RAW, m // RAW + 1)

            se.wait_ge(consts_ready, 4)
            link(nc.scalar.activation(dummy[:], dummy[:], ACT.Silu))
            se.wait_ge(vec_turned, 1)
            nc.scalar.activation(vt[:], pg[:, 0:VROWS], ACT.Copy).then_inc(pg_free, 1)
            se.wait_ge(pg_free, 1)
            nc.scalar.activation(cs[:, :, 0], vt[:, V_C:V_C + KT], ACT.Silu).then_inc(cs_ready, 1)
            nc.scalar.activation(cs[:, :, 1], vt[:, V_CC:V_CC + KT], ACT.Silu).then_inc(cs_ready, 1)

            se.wait_ge(consts_ready, 5)
            se.wait_ge(cs_ready, 2)
            nc.scalar.activation(csp[:, :, 0:2], cs[:], ACT.Copy).then_inc(csh_ready, 1)

            def square(stage, t, y_needed):
                k = stage * KT + t
                se.wait_ge(y_free, y_needed)
                if k >= 4:
                    se.wait_ge(ss_added, k - 3)
                ins = nc.scalar.activation(sq[:, t % 4, 0:LAT], xl[:, t, :], ACT.Square)
                if stage < 2:
                    ins = nc.scalar.activation(sq[:, t % 4, LAT:TOK], xc[:, t, :], ACT.Square)
                ins.then_inc(sq_ready, 1)

            def squares(stage, s, y0):
                for k in range(4 * (s - 2 * GROUP), 4 * (s - 2 * GROUP) + 4):
                    square(stage, k, y0 + k + 1)

            def roots(stage):
                for part in range(2 if stage < 2 else 1):
                    b = (pb, pa)[part]
                    se.wait_ge(ss_done, ROOTS[stage] + part + 1)
                    nc.scalar.activation(rms[:, part * LAT:(part + 1) * LAT], b[:, 0:LAT], ACT.Sqrt, bias=eps[:, 0:1],
                                         scale=1.0 / D).then_inc(rms_ready, 1)

            def modulate(stage, part, shift):
                o = part * LAT
                for t in range(KT):
                    se.wait_ge(nt_ready, TILES[stage] - KT + part * KT + t + 1)
                    nc.scalar.activation(hh[:, t, o:o + LAT], nt[:, t % 2, o:o + LAT], ACT.Identity,
                                         bias=shift[:, t:t + 1]).then_inc(hh_ready, 1)

            def group(i, ffn, m0, n, stage=None):
                for s in range(GSLABS):
                    q = s // 2
                    g = i * GROUP + (ffn * GROUPS * GROUP + q)
                    if s < 2 * GROUP and s % 2 == 0:
                        se.wait_ge(slab_used, i * GSLABS + (m0 + s + 1))
                        se.wait_ge(pu_free, g + 1)
                        nc.scalar.activation(sg[:, 0:n], pg[:, 0:n], ACT.Silu).then_inc(pg_free, 1)
                    m = m0 + s + 2
                    if stage is not None and s == GSLABS - 1:
                        squares(stage, s, (Y_F2 if ffn else Y_F1) + i * KT)
                    if not (isinstance(i, int) and i * GSLABS + m >= SLABS):
                        split(i * GSLABS + m, m % RAW, i * 3 + (m // RAW + 1))
                    if stage is not None and 2 * GROUP <= s < GSLABS - 1:
                        squares(stage, s, (Y_F2 if ffn else Y_F1) + i * KT)
                    if s < 2 * GROUP and s % 2 == 1:
                        se.wait_ge(pu_free, g + 2)
                        nc.scalar.activation(ah[:, q, 0:n], act[:, 0:n], ACT.Copy).then_inc(ah_ready, 1)

            def rows_out(i):
                se.wait_ge(slab_used, i * KT + KT)
                for q in range(4):
                    ins = nc.scalar.activation(rows[:, q * 512:(q + 1) * 512], py[q][0:4, :], ACT.Copy)
                ins.then_inc(rows_ready, 1)

            for t in range(KT):
                static_split(t)
                square(0, t, t + 1)
            roots(0)
            rows_out(0)
            for t in range(KT):
                static_split(KT + t)
            se.wait_ge(rows_turned, 1)
            rows_out(1)
            se.wait_ge(mods_ready, 2)
            for t in range(KT):
                static_split(2 * KT + t)
                if t >= 2:
                    se.wait_ge(hl_ready, t - 1)
                se.wait_ge(xr_ready, t + 1)
                nc.scalar.activation(hf[:, t % 2, LAT:TOK], xr[:, t, LAT:TOK], ACT.Identity, bias=mc[:, t:t + 1],
                                     scale=a1c[:, t:t + 1]).then_inc(hf_ready, 1)
                se.wait_ge(hf_ready, 2 * t + 2)
                nc.scalar.activation(hh[:, t, :], hf[:, t % 2, :], ACT.Copy).then_inc(hh_ready, 1)
            se.wait_ge(rows_turned, 2)
            rows_out(2)
            link(nc.scalar.activation(dummy[:], dummy[:], ACT.Silu))
            static_split(FFN1_0)
            static_split(FFN1_0 + 1)
            with se.Fori(0, GROUPS - 1) as i:
                group(i, 0, FFN1_0, TOK)
            group(GROUPS - 1, 0, FFN1_0, TOK, 1)
            roots(1)
            modulate(1, 0, ml[:, 3 * KT:4 * KT])
            modulate(1, 1, mc[:, 3 * KT:4 * KT])

            def project(s, out_ap, in_ap, func=ACT.Copy):
                se.wait_ge(slab_used, MIX0 + s + 1)
                nc.scalar.activation(out_ap, in_ap, func).then_inc(proj_free, 1)

            for j in range(HEADS):
                project(S_RG + j, rg[:, j, :], py[(S_RG + j) % 4][:, 0:LAT], ACT.Silu)
                static_split(MIX0 + S_RG + j + 2)
            for j in range(QT):
                project(S_CQ + j, cq[:, j, :], py[(S_CQ + j) % 4][:, 0:LAT])
                static_split(MIX0 + S_CQ + j + 2)
            for j in range(4):
                project(S_RQ + j, rq[:, j, :], py[(S_RQ + j) % 4][:, 0:LAT])
                static_split(MIX0 + S_RQ + j + 2)
            for j in range(CT):
                project(S_CKV + j, ckv[:, j, :], py[(S_CKV + j) % 4][:])
                static_split(MIX0 + S_CKV + j + 2)
            project(S_KR, krope[:], py[S_KR % 4][:])
            static_split(MIX0 + S_KR + 2)
            for j in range(4):
                project(S_RK + j, rk[:, j, :], py[(S_RK + j) % 4][:])
                static_split(MIX0 + S_RK + j + 2)
            for half in range(2):
                for k in range(4):
                    static_split(MIX0 + S_RV + 4 * half + k + 2)
                se.wait_ge(slab_used, MIX0 + S_RV + 4 * half + 4)
                for k in range(4):
                    s = S_RV + 4 * half + k
                    project(s, rv[:, k, half * 512:(half + 1) * 512], py[s % 4][:])

            se.wait_ge(lnu_ready, 1)
            nc.scalar.activation(lt[:, 1, :], lt[:, 0, :], ACT.Exp, scale=-1.0).then_inc(lnu_ready, 1)

            se.wait_ge(slab_used, MIX0 + S_UQ)
            nc.scalar.activation(lsq[:], cq[:].rearrange("p a b -> p (a b)"), ACT.Square).then_inc(lsq_ready, 1)
            se.wait_ge(lss_done, 1)
            nc.scalar.activation(rms[:, 0:LAT], pg[:, 0:LAT], ACT.Sqrt, bias=eps[:, 0:1], scale=1.0 / (QT * P)).then_inc(lrms_ready, 1)
            nc.scalar.activation(lsq[:], ckv[:].rearrange("p a b -> p (a b)"), ACT.Square).then_inc(lsq_ready, 1)
            se.wait_ge(lss_done, 2)
            se.wait_ge(lat_normed, 1)
            nc.scalar.activation(rms[:], pu[:], ACT.Sqrt, bias=eps[:, 0:1], scale=1.0 / (CT * P)).then_inc(lrms_ready, 1)

            def decays(h):
                se.wait_ge(darg_ready, h + 1)
                nc.scalar.activation(decay[:, h % 2, 0:2, :], decay[:, h % 2, 0:2, :], ACT.Exp)
                nc.scalar.activation(decay[:, h % 2, 2:4, :], far[:, 0, 2:4, :], ACT.Exp, scale=lg[:, h:h + 1])
                nc.scalar.activation(dback[:, h % 2], far[:, 1, 2:4, :], ACT.Exp, scale=lg[:, HEADS + h:HEADS + h + 1]).then_inc(decay_ready, 1)

            se.wait_ge(far_loaded, 16)
            decays(0)
            decays(1)
            for h in range(HEADS):
                if h + 2 < HEADS:
                    decays(h + 2)
                se.wait_ge(ry_done, h + 1)
                nc.scalar.activation(yret[:, h, :], pab[h % 2][:, 0:LAT], ACT.Copy).then_inc(ry_free, 1)
            se.wait_ge(lat_normed, 2)
            nc.scalar.activation(cqh[:], cq[:], ACT.Copy).then_inc(cqh_ready, 1)
            nc.scalar.activation(ckvh[:], ckv[:], ACT.Copy).then_inc(cqh_ready, 1)
            def y_square(k):
                se.wait_ge(yc_ready, k + 1)
                nc.scalar.activation(ysq[:, k % 2, :], yret[:, 2 * k:2 * k + 2, :].rearrange("p a b -> p (a b)"), ACT.Square).then_inc(ysq_ready, 1)

            def y_root(k):
                se.wait_ge(var_done, k + 1)
                nc.scalar.activation(ysd[:, k % 2, :], pab[k % 2][:], ACT.Sqrt, bias=eps[:, 1:2], scale=1.0 / P).then_inc(ysd_ready, 1)

            def y_high(k):
                se.wait_ge(yn_ready, k + 1)
                nc.scalar.activation(mixh[:, 2 * k:2 * k + 2, :], yret[:, 2 * k:2 * k + 2, :], ACT.Copy).then_inc(mixh_ready, 1)

            up_slabs = [4, 8, 12, 20, 28]

            def up(k, out_ap, in_ap):
                if k + 1 in up_slabs:
                    se.wait_ge(slab_used, MIX0 + S_UQ + up_slabs.index(k + 1) + 1)
                else:
                    se.wait_ge(up_done, k + 1 - sum(e <= k for e in up_slabs))
                nc.scalar.activation(out_ap, in_ap, ACT.Copy).then_inc(up_free, 1)

            def up_queries(half):
                for h in range(4 * half, 4 * half + 4):
                    up(h, qn[:, h, :], py[h % 4][:, 0:LAT])
                static_split(MIX0 + S_UQ + half + 2)

            y_square(0)
            y_square(1)
            up_queries(0)
            y_root(0)
            y_square(2)
            y_root(1)
            y_square(3)
            y_high(0)
            up_queries(1)
            y_high(1)
            y_root(2)
            y_root(3)
            for j in range(4):
                up(8 + j, qr[:, j, :], py[j % 4][:, 0:LAT])
            static_split(MIX0 + S_UQ + 4)
            y_high(2)
            y_high(3)
            for h in range(HEADS):
                up(12 + h, kn[:, h, :], py[h % 4][:])
            static_split(MIX0 + S_UQ + 5)
            se.wait_ge(mixl_ready, 4)
            for k in range(4):
                for half in range(2):
                    j = 20 + 2 * k + half
                    up(j, vm[half][:, k, :], py[j % 4][:])
            static_split(MIX0 + S_UQ + 6)

            def exps(a):
                se.wait_ge(nm_ready, a + 1)
                if a >= 2:
                    se.wait_ge(turned, a - 1)
                nc.scalar.activation(pn[:, a % 2, :], py[a % 3][:], ACT.Exp, bias=nm[:, a:a + 1], scale=MLA_SCALE,
                                     accum_out=rsum[:, a:a + 1]).then_inc(exp_done, 1)

            def probs(a):
                h, k = a // 2, a % 2
                se.wait_ge(turned, a + 1)
                if h >= 2 and k == 0:
                    se.wait_ge(o_done, h - 1)
                nc.scalar.activation(pt[h % 2][:, :, k * P:(k + 1) * P], pgu[a % 2][:].rearrange("p (j q) -> p j q", q=P),
                                     ACT.Copy).then_inc(pt_ready, 1)

            def out_high(h):
                se.wait_ge(o_done, h + 1)
                nc.scalar.activation(mixh[:, HEADS + h, :], pab[h % 2][:, 0:LAT], ACT.Copy).then_inc(oh_ready, 1)

            exps(0)
            exps(1)
            for a in range(16):
                probs(a)
                if a + 2 < 16:
                    exps(a + 2)
                if a % 2 == 1 and a > 1:
                    out_high(a // 2 - 1)
                    static_split(MIX0 + S_OUTR + a // 2 + 1)
            out_high(HEADS - 1)
            static_split(MIX0 + S_OUTM + 1)

            for s in range(8):
                if s < 7:
                    static_split(MIX0 + S_OUTM + s + 2)
                for t in (2 * s, 2 * s + 1):
                    square(2, t, Y_OUT + HEADS + s + 1)
            roots(2)
            static_split(FFN2_0 + 1)
            modulate(2, 0, ml[:, 6 * KT:7 * KT])
            link(nc.scalar.activation(dummy[:], dummy[:], ACT.Silu))
            with se.Fori(0, GROUPS - 1) as i:
                group(i, 1, FFN2_0, LAT)
            group(GROUPS - 1, 1, FFN2_0, LAT, 3)
            roots(3)
            for q in range(4):
                for k in range(2):
                    j = 2 * q + k
                    se.wait_ge(turned, 16 + j + 1)
                    nc.scalar.activation(outn[:, k, q * 512:(q + 1) * 512], py[j % 4][:], ACT.Copy).then_inc(out_ready, 1)

        @block.tensor
        def _(pe):
            mm = nc.tensor.matmul
            ident = eyes[:, 0, :]

            def three(out_ap, w, xh_ap, xl_ap, first, last):
                mm(out_ap, w[0], xh_ap, start=first, stop=False, skip_group_check=True)
                mm(out_ap, w[0], xl_ap, start=False, stop=False, skip_group_check=True)
                return mm(out_ap, w[1], xh_ap, start=False, stop=last, skip_group_check=True)

            pe.wait_ge(vec_loaded, 16 * 10)
            nc.tensor.transpose(pg[:, 0:VROWS], vnat[:, :], ident[0:VROWS, 0:VROWS])
            nc.tensor.transpose(pu[:, 0:72], bnat[:, 0, :], ident[0:72, 0:72])
            nc.tensor.transpose(pa[:, 0:72], bnat[:, 1, :], ident[0:72, 0:72]).then_inc(vec_turned, 1)
            pe.wait_ge(x_loaded, 4 * 16)
            for t in range(KT):
                if t >= 4:
                    pe.wait_ge(y_free, t - 3)
                for k in range(4):
                    ins = nc.tensor.transpose(py[t % 4][:, k * P:(k + 1) * P], xnat[:, k, t * P:(t + 1) * P], ident)
                ins.then_inc(x_turned, 1)

            def square_sums(stage):
                pe.wait_ge(ss_added, (stage + 1) * KT)
                mm(pb[:, 0:LAT], ones[:], ssum[:, 0:LAT], start=True, stop=True).then_inc(ss_done, 1)
                if stage < 2:
                    mm(pa[:, 0:LAT], ones[:], ssum[:, LAT:TOK], start=True, stop=True).then_inc(ss_done, 1)

            pe.wait_ge(consts_ready, 5)
            pe.wait_ge(pa_free, 1)

            pe.wait_ge(csl_ready, 1)
            for i in range(3):
                if i:
                    pe.wait_ge(rows_ready, i)
                for t in range(KT):
                    m = i * KT + t
                    pe.wait_ge(wl_ready, m + 1)
                    for q in range(4):
                        mm(py[q][:], csp[:, t, :], wh[:, m % 2, q * 512:(q + 1) * 512], start=(t == 0), stop=False)
                        ins = mm(py[q][:], csp[:, t, :], wl[:, m % 2, q * 512:(q + 1) * 512], start=False, stop=(t == KT - 1))
                    ins.then_inc(slab_used, 1)
                if i == 0:
                    square_sums(0)
                    pe.wait_ge(rms_ready, 2)
                pe.wait_ge(rows_ready, i + 1)
                if i:
                    pe.wait_ge(pa_free, i + 1)
                for j in range(KT):
                    ins = nc.tensor.transpose(pa[:, 4 * j:4 * j + 4], rows[:, j * P:(j + 1) * P], ident[0:4, 0:4])
                ins.then_inc(rows_turned, 1)

            def w_at(m, a, b):
                return (slab_at(wh, m, a, b), slab_at(wl, m, a, b))

            def column_slab(m, bank_ap, n, rhs_h, rhs_l, first_tile=None):
                for t in range(KT):
                    if first_tile is not None:
                        pe.wait_ge(hl_ready, first_tile + t + 1)
                    ins = three(bank_ap[:, 0:n], w_at(m, t * P, (t + 1) * P), rhs_h[:, t, 0:n], rhs_l[:, t, 0:n],
                                t == 0, t == KT - 1)
                return ins

            def turn_sums(v, chunks, a):
                pe.wait_ge(chunk_free, chunks + 2)
                pe.wait_ge(pa_free, v + 4)
                for j in range(8):
                    ins = nc.tensor.transpose((pa, pb)[j // 4][:, (j % 4) * P:(j % 4 + 1) * P], a[:, j * P:(j + 1) * P], ident)
                ins.then_inc(ada_summed, 1)

            def group(i, ffn, m0, n, units=None):
                y0 = Y_F2 if ffn else Y_F1
                for s in range(GSLABS):
                    if units == 1 and s == 9:
                        turn_sums(i * 2, i * KT + KT, accl)
                    if units == 1 and s == 10:
                        turn_sums(i * 2 + 1, i * KT + KT, accc)
                    if units == 2 and s == 5:
                        turn_sums(i * 2, (i - 4) * (2 * KT) + 5 * KT, accl)
                    if units == 2 and s == 10:
                        turn_sums(i * 2 + 1, (i - 4) * (2 * KT) + 6 * KT, accl)
                    pe.wait_ge(wl_ready, i * GSLABS + (m0 + s + 1))
                    if s < 2 * GROUP:
                        g = i * GROUP + (ffn * GROUPS * GROUP + s // 2)
                        free, b = ((pg_free, pg), (pu_free, pu))[s % 2]
                        pe.wait_ge(free, g + 1)
                        column_slab(s, b, n, hh, hl, (3 * KT if ffn else 0) if s == 0 else None).then_inc(slab_used, 1)
                    else:
                        dq = s - 2 * GROUP
                        for part in ((0, 3), (3, 4)) if dq == 0 else ((0, 4),):
                            if part[1] == 4:
                                pe.wait_ge(al_ready, i * GROUP + (ffn * GROUPS * GROUP + 5))
                            else:
                                pe.wait_ge(al_ready, i * GROUP + (ffn * GROUPS * GROUP + 4))
                            for d in range(4):
                                if part[0] == 0:
                                    pe.wait_ge(y_free, i * KT + (y0 + dq * 4 + d - 3))
                                for q in range(*part):
                                    ins = three(py[d][:, 0:n], w_at(s, q * 512 + d * P, q * 512 + (d + 1) * P),
                                                ah[:, q, 0:n], al[:, q, 0:n], q == 0, q == 3)
                                if part[1] == 4:
                                    ins.then_inc(y_done if d < 3 else slab_used, 1)

            pe.wait_ge(rows_ready, 3)
            with pe.Fori(0, 4) as i:
                group(i, 0, FFN1_0, TOK, 1)
            with pe.Fori(4, 8) as i:
                group(i, 0, FFN1_0, TOK, 2)
            with pe.Fori(8, GROUPS) as i:
                group(i, 0, FFN1_0, TOK)
            square_sums(1)

            pe.wait_ge(wl_ready, MIX0 + 2)
            for t in range(KT):
                pe.wait_ge(hl_ready, TILES[1] + t + 1)
                for s in range(2):
                    ins = three(py[s][:, 0:LAT], w_at(s, t * P, (t + 1) * P), hh[:, t, 0:LAT], hl[:, t, 0:LAT],
                                t == 0, t == KT - 1)
                    if t == KT - 1:
                        ins.then_inc(slab_used, 1)

            def proj(s, b, n, i=0):
                pe.wait_ge(wl_ready, i * 4 + (MIX0 + s + 1))
                if not (isinstance(i, int) and s < 4):
                    pe.wait_ge(proj_free, i * 4 + (s - 3))
                column_slab(s, py[b], n, hh, hl).then_inc(slab_used, 1)

            proj(2, 2, LAT)
            proj(3, 3, LAT)
            with pe.Fori(0, 3) as i:
                for s in range(4, 8):
                    proj(s, s % 4, LAT, i)
            pe.wait_ge(hl_ready, TILES[2])
            for s in range(S_CKV, S_RV):
                proj(s, s % 4, TOK)
            with pe.Fori(0, 2) as half:
                for q in range(4):
                    s = S_RV + q
                    pe.wait_ge(wl_ready, half * 4 + (MIX0 + s + 1))
                    for k in range(4):
                        if q == 0:
                            pe.wait_ge(proj_free, half * 4 + (S_RV + k - 3))
                        o = py[(S_RV + k) % 4][:]
                        for j in range(4):
                            t = 4 * q + j
                            w_h, w_l = w_at(s, j * 512, (j + 1) * 512)
                            xh_ap, xl_ap = hh[:, t, k * P:(k + 1) * P], hl[:, t, k * P:(k + 1) * P]
                            mm(o, xh_ap, w_h, start=(t == 0), stop=False)
                            mm(o, xl_ap, w_h, start=False, stop=False)
                            ins = mm(o, xh_ap, w_l, start=False, stop=(t == KT - 1))
                    ins.then_inc(slab_used, 1)

            pe.wait_ge(lsq_ready, 1)
            for t in range(QT):
                ins = mm(pg[:, 0:LAT], ones[:], lsq[:, t * LAT:(t + 1) * LAT], start=(t == 0), stop=(t == QT - 1))
            ins.then_inc(lss_done, 1)
            pe.wait_ge(lsq_ready, 2)
            for t in range(CT):
                ins = mm(pu[:], ones[:], lsq[:, t * TOK:(t + 1) * TOK], start=(t == 0), stop=(t == CT - 1))
            ins.then_inc(lss_done, 1)

            def swap(r, src, perm):
                if r == 0:
                    pe.wait_ge(lrms_ready, 1)
                elif r == 1:
                    pe.wait_ge(lrms_ready, 2)
                else:
                    pe.wait_ge(rope_done, r - 1)
                mm(pgu[r % 2][:, 0:LAT], eyes[:, perm, :], src, start=True, stop=True).then_inc(swapped, 1)

            pe.wait_ge(proj_free, S_UQ)
            for j in range(4):
                swap(j, rq[:, j, :], 1)
            for j in range(4):
                swap(4 + j, rk[:, j, 0:LAT], 1)
            swap(8, krope[:, 0:LAT], 2)

            def ret_scores(h):
                if h >= 2:
                    pe.wait_ge(rp_ready, h - 1)
                lo = (h % 2) * DK
                for j in range(4):
                    ins = mm(py[2 * (h % 2) + j // 2][:, (j % 2) * LAT:(j % 2 + 1) * LAT],
                             rk[lo:lo + DK, h // 2, j * P:(j + 1) * P], rq[lo:lo + DK, h // 2, :],
                             start=(j % 2 == 0), stop=True, skip_group_check=True)
                ins.then_inc(rs_done, 1)

            def ret_values(h):
                pe.wait_ge(rp_ready, h + 1)
                if h >= 2:
                    pe.wait_ge(ry_free, h - 1)
                for j in range(4):
                    ins = mm(pab[h % 2][:, 0:LAT], rv[:, j, h * P:(h + 1) * P], pret[:, h % 2, j, :],
                             start=(j == 0), stop=(j == 3))
                ins.then_inc(ry_done, 1)

            pe.wait_ge(rope_done, 9)
            ret_scores(0)
            for h in range(HEADS):
                if h + 1 < HEADS:
                    ret_scores(h + 1)
                ret_values(h)

            def y_mean(k):
                if k == 0:
                    pe.wait_ge(ry_free, HEADS)
                if k >= 2:
                    pe.wait_ge(yc_ready, k - 1)
                mm(pgu[k % 2][:], ones[:], yret[:, 2 * k:2 * k + 2, :].rearrange("p a b -> p (a b)"), start=True, stop=True).then_inc(mu_done, 1)

            def y_var(k):
                pe.wait_ge(ysq_ready, k + 1)
                if k >= 2:
                    pe.wait_ge(ysd_ready, k - 1)
                mm(pab[k % 2][:], ones[:], ysq[:, k % 2, :], start=True, stop=True).then_inc(var_done, 1)

            def up_bank(k):
                if k >= 4:
                    pe.wait_ge(up_free, k - 3)
                return py[k % 4]

            def up_queries(which):
                m = MIX0 + S_UQ + which
                pe.wait_ge(wl_ready, m + 1)
                for j in range(4):
                    b = up_bank(4 * which + j)
                    for t in range(QT):
                        ins = three(b[:, 0:LAT], w_at(m, t * 512 + j * P, t * 512 + (j + 1) * P), cqh[:, t, :], cql[:, t, :],
                                    t == 0, t == QT - 1)
                    ins.then_inc(up_done if j < 3 else slab_used, 1)

            y_mean(0)
            y_mean(1)
            pe.wait_ge(lat_split, 2)
            up_queries(0)
            y_var(0)
            y_mean(2)
            y_var(1)
            y_mean(3)
            up_queries(1)
            y_var(2)
            y_var(3)
            up_queries(2)
            m = MIX0 + S_UKV
            pe.wait_ge(wl_ready, m + 1)
            for h in range(HEADS):
                b = up_bank(12 + h)
                for t in range(CT):
                    ins = three(b[:], w_at(m, t * 1024 + h * P, t * 1024 + (h + 1) * P), ckvh[:, t, :], ckvl[:, t, :],
                                t == 0, t == CT - 1)
                ins.then_inc(up_done if h < HEADS - 1 else slab_used, 1)
            m = MIX0 + S_UKV + 1
            pe.wait_ge(wl_ready, m + 1)
            for k in range(4):
                for half in range(2):
                    b = up_bank(20 + 2 * k + half)
                    for t in range(CT):
                        w_h, w_l = w_at(m, t * 1024 + half * 512, t * 1024 + (half + 1) * 512)
                        xh_ap, xl_ap = ckvh[:, t, k * P:(k + 1) * P], ckvl[:, t, k * P:(k + 1) * P]
                        mm(b[:], xh_ap, w_h, start=(t == 0), stop=False)
                        mm(b[:], xl_ap, w_h, start=False, stop=False)
                        ins = mm(b[:], xh_ap, w_l, start=False, stop=(t == CT - 1))
                    ins.then_inc(up_done if (k, half) != (3, 1) else slab_used, 1)
            pe.wait_ge(up_free, 12)
            for j in range(4):
                if j == 0:
                    pe.wait_ge(yc_ready, 4)
                swap(9 + j, qr[:, j, :], 2)

            def scores(a):
                h, k = a // 2, a % 2
                if a >= 3:
                    pe.wait_ge(exp_done, a - 2)
                lo = (h % 2) * ROPE
                b = py[a % 3]
                mm(b[:], qn[:, h, k * P:(k + 1) * P], kn[:, h, :], start=True, stop=False)
                mm(b[:], qr[lo:lo + ROPE, h // 2, k * P:(k + 1) * P], krope[lo:lo + ROPE, :], start=False, stop=True).then_inc(sc_done, 1)

            def turn(a):
                pe.wait_ge(pn_ready, a + 1)
                if a >= 2:
                    pe.wait_ge(pt_ready, a - 1)
                for j in range(4):
                    ins = nc.tensor.transpose(pgu[a % 2][:, j * P:(j + 1) * P], pn[:, a % 2, j * P:(j + 1) * P], ident)
                ins.then_inc(turned, 1)

            def values(h):
                pe.wait_ge(pt_ready, 2 * h + 2)
                if h >= 2:
                    pe.wait_ge(ol_ready, h - 1)
                for j in range(4):
                    ins = mm(pab[h % 2][:, 0:LAT], vm[h // 4][:, j, (h % 4) * P:(h % 4 + 1) * P], pt[h % 2][:, j, :], start=(j == 0), stop=(j == 3))
                ins.then_inc(o_done, 1)

            def out_slab(m, b, head0):
                for d in range(2):
                    for k in range(HEADS):
                        ins = three(b[:, d * LAT:(d + 1) * LAT], w_at(m, k * LAT + d * P, k * LAT + (d + 1) * P),
                                    mixh[:, head0 + k, :], mixl[:, head0 + k, :], k == 0 and d == 0, k == HEADS - 1)
                ins.then_inc(slab_used, 1)

            pe.wait_ge(up_free, 28)
            pe.wait_ge(rope_done, 13)
            scores(0)
            scores(1)
            for a in range(16):
                if a + 2 < 16:
                    scores(a + 2)
                turn(a)
                if a % 2 == 1:
                    values(a // 2)
                    h = a // 2
                    pe.wait_ge(wl_ready, MIX0 + S_OUTR + h + 1)
                    pe.wait_ge(y_free, Y_OUT + h)
                    out_slab(MIX0 + S_OUTR + h, py[3], 0)

            pe.wait_ge(ol_ready, HEADS)
            with pe.Fori(0, 2) as i:
                for s in range(4):
                    pe.wait_ge(wl_ready, i * 4 + (MIX0 + S_OUTM + s + 1))
                    pe.wait_ge(y_free, i * 4 + (Y_OUT + HEADS + s - 3))
                    out_slab(MIX0 + S_OUTM + s, py[s], HEADS)
            square_sums(2)
            with pe.Fori(0, GROUPS) as i:
                group(i, 1, FFN2_0, LAT)
            square_sums(3)
            pe.wait_ge(fin_ready, KT)
            for q in range(4):
                for k in range(2):
                    j = 2 * q + k
                    if j >= 4:
                        pe.wait_ge(out_ready, j - 3)
                    for t in range(4):
                        ins = nc.tensor.transpose(py[j % 4][:, t * P:(t + 1) * P], xl[:, 4 * q + t, k * P:(k + 1) * P], ident)
                    ins.then_inc(turned, 1)

        @block.vector
        def _(ve):
            tt = nc.vector.tensor_tensor
            ts = nc.vector.tensor_scalar
            stt = nc.vector.scalar_tensor_tensor
            count = [0]

            def link(ins):
                count[0] += 1
                ins.then_inc(dve_chain, 1)
                ve.wait_ge(dve_chain, count[0])

            def split(m, slot):
                ve.wait_ge(wh_ready, m + 1)
                tt(wl[:, slot % 2, :], raw[:, slot, :], wh[:, slot % 2, :].bitcast(F32), ALU.subtract).then_inc(wl_ready, 1)

            def static_split(m):
                if m < SLABS:
                    split(m, m % RAW)

            link(nc.vector.memset(mx[:], 0.0))
            nc.vector.memset(rrec[:], 0.0).then_inc(al_ready, 1)
            ve.wait_ge(vec_turned, 1)
            nc.vector.tensor_copy(bt[:, 0:72], pu[:, 0:72]).then_inc(pu_free, 1)
            nc.vector.tensor_copy(bt[:, 72:144], pa[:, 0:72]).then_inc(pa_free, 1)
            def input_tile(t):
                ve.wait_ge(x_turned, t + 1)
                nc.vector.tensor_copy(xl[:, t, :], py[t % 4][:, 0:LAT])
                nc.vector.tensor_copy(xc[:, t, :], py[t % 4][:, LAT:TOK]).then_inc(y_free, 1)

            def square_add(stage, t):
                n = TOK if stage < 2 else LAT
                ve.wait_ge(sq_ready, stage * KT + t + 1)
                if t == 0:
                    ins = nc.vector.tensor_copy(ssum[:, 0:n], sq[:, 0, 0:n])
                else:
                    ve.wait_ge(ss_added, stage * KT + t)
                    ins = tt(ssum[:, 0:n], ssum[:, 0:n], sq[:, t % 4, 0:n], ALU.add)
                ins.then_inc(ss_added, 1)

            def roots(stage, part):
                ve.wait_ge(rms_ready, ROOTS[stage] + part + 1)
                o = part * LAT
                link(nc.vector.reciprocal(rms[:, o:o + LAT], rms[:, o:o + LAT]))

            def modulation(i):
                ve.wait_ge(rows_turned, i + 1)
                sums = pa[:, 0:4 * KT].rearrange("p (j k) -> p k j", k=4)
                lo = i * KT
                for k, m in enumerate((ml, mc)):
                    link(tt(m[:, lo:lo + KT], sums[:, k, :], bt[:, lo:lo + KT], ALU.add))
                    ins = tt(m[:, lo:lo + KT], sums[:, 2 + k, :], m[:, lo:lo + KT], ALU.add)
                    if k:
                        ins.then_inc(pa_free, 1)
                    else:
                        link(ins)

            def amp(dst, mod, m, g):
                link(stt(dst[:], m[:, mod * KT:(mod + 1) * KT], 1.0, vt[:, g:g + KT], ALU.add, ALU.mult))

            def scaled(k, t, src, a, o):
                if t >= 2:
                    ve.wait_ge(hl_ready, k - 1)
                stt(nt[:, t % 2, o:o + LAT], src[:, t, :], a[:, t:t + 1], rms[:, o:o + LAT], ALU.mult, ALU.mult).then_inc(nt_ready, 1)

            def modulate(stage, part, src, a, shift):
                o = part * LAT
                k0 = TILES[stage] + part * KT
                scaled(k0, 0, src, a, o)
                for t in range(KT):
                    if t + 1 < KT:
                        scaled(k0 + t + 1, t + 1, src, a, o)
                    ve.wait_ge(hh_ready, k0 + t + 1)
                    stt(hl[:, t, o:o + LAT], nt[:, t % 2, o:o + LAT], shift[:, t:t + 1], hh[:, t, o:o + LAT].bitcast(F32),
                        ALU.add, ALU.subtract).then_inc(hl_ready, 1)

            for t in range(KT):
                input_tile(t)
            ve.wait_ge(csh_ready, 1)
            tt(csp[:, :, 2:4], cs[:], csp[:, :, 0:2].bitcast(F32), ALU.subtract).then_inc(csl_ready, 1)
            for t in range(KT):
                static_split(t)
                square_add(0, t)
            roots(0, 0)
            roots(0, 1)
            ve.wait_ge(y_free, KT)
            for t in range(KT):
                static_split(KT + t)
                if t == 2:
                    modulation(0)
                tt(xr[:, t, 0:LAT], xl[:, t, :], rms[:, 0:LAT], ALU.mult)
                tt(xr[:, t, LAT:TOK], xc[:, t, :], rms[:, LAT:TOK], ALU.mult).then_inc(xr_ready, 1)
            modulation(1)
            ve.wait_ge(pa_free, 3)
            amp(a1l, 1, ml, V_N1)
            amp(a1c, 1, mc, V_N1)
            nc.vector.memset(nm[:], 0.0).then_inc(mods_ready, 2)
            for t in range(KT):
                static_split(2 * KT + t)
                ve.wait_ge(xr_ready, t + 1)
                if t >= 2:
                    ve.wait_ge(hl_ready, t - 1)
                ts(hf[:, t % 2, 0:LAT], xr[:, t, 0:LAT], a1l[:, t:t + 1], ml[:, t:t + 1], ALU.mult, ALU.add).then_inc(hf_ready, 1)
                ve.wait_ge(hh_ready, t + 1)
                tt(hl[:, t, :], hf[:, t % 2, :], hh[:, t, :].bitcast(F32), ALU.subtract).then_inc(hl_ready, 1)
            static_split(FFN1_0)
            static_split(FFN1_0 + 1)
            modulation(2)
            ve.wait_ge(pa_free, 4)
            link(ts(g1l[:], ml[:, 2 * KT:3 * KT], 0.5, None, ALU.mult))
            link(ts(g1c[:], mc[:, 2 * KT:3 * KT], 0.5, None, ALU.mult))
            nc.vector.memset(mx[:], 0.0).then_inc(chunk_free, 2)

            def group(i, ffn, m0, n, gates, units=None, stage=None):
                y0 = Y_F2 if ffn else Y_F1
                for s in range(GSLABS):
                    if s < 2 * GROUP:
                        q = s // 2
                        g = i * GROUP + (ffn * GROUPS * GROUP + q)
                        if s % 2:
                            ve.wait_ge(slab_used, i * GSLABS + (m0 + s + 1))
                            ve.wait_ge(pg_free, g + 2)
                            ve.wait_ge(al_ready, g + 1)
                            tt(act[:, 0:n], sg[:, 0:n], pu[:, 0:n], ALU.mult).then_inc(pu_free, 1)
                    else:
                        dq = s - 2 * GROUP
                        for d in range(4):
                            if d < 3:
                                ve.wait_ge(y_done, i * 12 + (ffn * GROUPS * 12 + dq * 3 + d + 1))
                            else:
                                ve.wait_ge(slab_used, i * GSLABS + (m0 + s + 1))
                            k = dq * 4 + d
                            ve.wait_ge(y_free, i * KT + (y0 + k - KT + 1))
                            for x_, gate, o in gates:
                                ins = stt(x_[:, k, :], py[d][:, o:o + LAT], gate[:, k:k + 1], x_[:, k, :], ALU.mult, ALU.add)
                            ins.then_inc(y_free, 1)
                    m = s + 2
                    if stage is not None and s == GSLABS - 1:
                        for k in range(KT - 4, KT):
                            square_add(stage, k)
                    if not (isinstance(i, int) and i * GSLABS + m0 + m >= SLABS):
                        split(i * GSLABS + (m0 + m), m % RAW)
                    if stage is not None and 2 * GROUP <= s < GSLABS - 1:
                        for k in range(4 * (s - 2 * GROUP), 4 * (s - 2 * GROUP) + 4):
                            square_add(stage, k)
                    if s < 2 * GROUP and s % 2:
                        ve.wait_ge(ah_ready, g + 1)
                        tt(al[:, q, 0:n], act[:, 0:n], ah[:, q, 0:n].bitcast(F32), ALU.subtract).then_inc(al_ready, 1)
                    if units == 1:
                        if s < 8:
                            for t in (2 * s, 2 * s + 1):
                                if t > 0:
                                    ve.wait_ge(chunk_free, i * KT + t + 2)
                                ve.wait_ge(chunk_loaded[t % 2], i * (8 * 16) + (t // 2 + 1) * 16)
                                chunk_ops(t, True)
                        if s in (9, 10):
                            column_sums(i * 2 + (s - 9), (ml, mc)[s - 9], i * 8 + 3 * KT)
                    if units == 2:
                        for half, lo in ((0, 0), (1, 5)):
                            if lo <= s < lo + 4:
                                for t in range(4 * (s - lo), 4 * (s - lo) + 4):
                                    if t > 0:
                                        ve.wait_ge(chunk_free, (i - 4) * (2 * KT) + (4 * KT + half * KT + t + 2))
                                    ve.wait_ge(chunk_loaded[t % 2], (i - 4) * (16 * 16) + (32 + 8 * half + t // 2 + 1) * 16)
                                    chunk_ops(t, False)
                            if s == (4, 10)[half]:
                                column_sums(i * 2 + half, ml, i * 16 + (8 * half - 32 + 3 * KT))

            def chunk_ops(t, with_ctx):
                for k, a in enumerate((accl, accc) if with_ctx else (accl,)):
                    if t == 0:
                        ins = ts(a[:], chunk[:, 0, :], cs[:, 0, k:k + 1], None, ALU.mult)
                    else:
                        ins = stt(a[:], chunk[:, t % 2, :], cs[:, t, k:k + 1], a[:], ALU.mult, ALU.add)
                ins.then_inc(chunk_free, 1)

            def column_sums(v, m, off):
                ve.wait_ge(ada_summed, v + 1)
                ve.wait_ge(pa_free, v + 4)
                for k, b in enumerate((pa, pb)):
                    ins = nc.vector.tensor_reduce(red[:, 4 * k:4 * k + 4], b[:].rearrange("p (j q) -> p j q", q=P), AX.X, ALU.add)
                ins.then_inc(red_ready, 1)
                ve.wait_ge(red_ready, v + 1)
                tt(m[:, ds(off, 8)], red[:], bt[:, ds(off, 8)], ALU.add).then_inc(pa_free, 1)

            gates1 = [(xl, g1l, 0), (xc, g1c, LAT)]
            with ve.Fori(0, 4) as i:
                group(i, 0, FFN1_0, TOK, gates1, 1)
            with ve.Fori(4, 8) as i:
                group(i, 0, FFN1_0, TOK, gates1, 2)
            with ve.Fori(8, GROUPS - 1) as i:
                group(i, 0, FFN1_0, TOK, gates1)
            ve.wait_ge(pa_free, 4 + 16)
            amp(a2l, 4, ml, V_N2)
            amp(a2c, 4, mc, V_N2)
            amp(a3l, 7, ml, V_N3)
            link(ts(g3l[:], ml[:, 8 * KT:9 * KT], 0.5, None, ALU.mult))
            group(GROUPS - 1, 0, FFN1_0, TOK, gates1, None, 1)
            roots(1, 0)
            modulate(1, 0, xl, a2l, ml[:, 3 * KT:4 * KT])
            roots(1, 1)
            modulate(1, 1, xc, a2c, mc[:, 3 * KT:4 * KT])

            for s in range(S_RG, S_RV):
                static_split(MIX0 + s + 2)
            for s in range(S_RV, S_UQ):
                static_split(MIX0 + s + 2)

            ve.wait_ge(rope_loaded, 3 * 16)
            link(ts(lt[:, 0, :], dec[:], -1.0, None, ALU.mult))
            tt(lt[:, 0, :], lt[:, 0, :], dec[:], ALU.max).then_inc(lnu_ready, 1)
            ve.wait_ge(lnu_ready, 2)
            link(ts(lt[:, 2, :], lt[:, 1, :], 2.0, None, ALU.add))
            link(nc.vector.reciprocal(lt[:, 2, :], lt[:, 2, :]))
            link(tt(lt[:, 2, :], lt[:, 2, :], lt[:, 1, :], ALU.mult))
            link(tt(lt[:, 3, :], lt[:, 2, :], lt[:, 2, :], ALU.mult))
            link(ts(lg[:], lt[:, 3, :], 1.0 / 17, None, ALU.mult))
            for k in (15, 13, 11, 9, 7, 5, 3):
                link(stt(lg[:], lg[:], 1.0 / k, lt[:, 3, :], ALU.add, ALU.mult))
            link(stt(lg[:], lg[:], 1.0, lt[:, 2, :], ALU.add, ALU.mult))
            link(ts(lt[:, 0, :], dec[:], 0.0, None, ALU.min))
            link(stt(lg[:], lg[:], -2.0, lt[:, 0, :], ALU.mult, ALU.add))

            ve.wait_ge(lrms_ready, 1)
            link(nc.vector.reciprocal(rms[:, 0:LAT], rms[:, 0:LAT]))
            for t in range(QT):
                ins = stt(cq[:, t, :], cq[:, t, :], vt[:, V_QG + t:V_QG + t + 1], rms[:, 0:LAT], ALU.mult, ALU.mult)
            ins.then_inc(lat_normed, 1)
            ve.wait_ge(lrms_ready, 2)
            link(nc.vector.reciprocal(rms[:], rms[:]))
            for t in range(CT):
                ins = stt(ckv[:, t, :], ckv[:, t, :], vt[:, V_KG + t:V_KG + t + 1], rms[:], ALU.mult, ALU.mult)
            ins.then_inc(lat_normed, 1)

            def rotate(r, tile, tab):
                ve.wait_ge(swapped, r + 1)
                link(tt(rope_t[:], pgu[r % 2][:, 0:LAT], ropes[:, tab + 1, :], ALU.mult))
                link(tt(tile, tile, ropes[:, tab, :], ALU.mult))
                tt(tile, tile, rope_t[:], ALU.add).then_inc(rope_done, 1)
                ve.wait_ge(rope_done, r + 1)

            for j in range(4):
                rotate(j, rq[:, j, :], 0)
            for j in range(4):
                rotate(4 + j, rk[:, j, 0:LAT], 0)
            rotate(8, krope[:, 0:LAT], 2)

            def decay_arg(h):
                d = decay[:, h % 2, 0:2, :]
                link(ts(d, far[:, 1, 0:2, :], lg[:, HEADS + h:HEADS + h + 1], None, ALU.mult))
                stt(d, far[:, 0, 0:2, :], lg[:, h:h + 1], d, ALU.mult, ALU.add).then_inc(darg_ready, 1)

            ve.wait_ge(far_loaded, 16)
            decay_arg(0)
            decay_arg(1)
            for h in range(HEADS):
                ve.wait_ge(decay_ready, h + 1)
                link(tt(decay[:, h % 2, 2:4, :], decay[:, h % 2, 2:4, :], dback[:, h % 2], ALU.add))
                ve.wait_ge(rs_done, h + 1)
                if h >= 2:
                    ve.wait_ge(ry_done, h - 1)
                for j in range(2):
                    ins = stt(pret[:, h % 2, 2 * j:2 * j + 2, :], py[2 * (h % 2) + j][:].rearrange("p (a b) -> p a b", a=2),
                              float(DK) ** -0.5, decay[:, h % 2, 2 * j:2 * j + 2, :], ALU.mult, ALU.mult)
                ins.then_inc(rp_ready, 1)
                if h + 2 < HEADS:
                    ve.wait_ge(rp_ready, h + 1)
                    decay_arg(h + 2)
            ve.wait_ge(cqh_ready, 1)
            tt(cql[:], cq[:], cqh[:].bitcast(F32), ALU.subtract).then_inc(lat_split, 1)
            ve.wait_ge(cqh_ready, 2)
            tt(ckvl[:], ckv[:], ckvh[:].bitcast(F32), ALU.subtract).then_inc(lat_split, 1)

            def two(t, k):
                return t[:, 2 * k:2 * k + 2, :].rearrange("p a b -> p (a b)")

            def center(k):
                ve.wait_ge(mu_done, k + 1)
                stt(two(yret, k), pgu[k % 2][:], -1.0 / P, two(yret, k), ALU.mult, ALU.add).then_inc(yc_ready, 1)

            def y_low(k):
                ve.wait_ge(mixh_ready, k + 1)
                tt(two(mixl, k), two(yret, k), two(mixh, k).bitcast(F32), ALU.subtract).then_inc(mixl_ready, 1)

            def y_norm(k):
                ve.wait_ge(ysd_ready, k + 1)
                link(nc.vector.reciprocal(ysd[:, k % 2, :], ysd[:, k % 2, :]))
                link(tt(two(yret, k), two(yret, k), ysd[:, k % 2, :], ALU.mult))
                tt(two(yret, k), two(yret, k), two(rg, k), ALU.mult).then_inc(yn_ready, 1)

            center(0)
            center(1)
            static_split(MIX0 + S_UQ + 2)
            y_norm(0)
            center(2)
            y_norm(1)
            center(3)
            y_low(0)
            static_split(MIX0 + S_UQ + 3)
            y_low(1)
            y_norm(2)
            y_norm(3)
            static_split(MIX0 + S_UQ + 4)
            y_low(2)
            y_low(3)
            static_split(MIX0 + S_UQ + 5)
            static_split(MIX0 + S_UQ + 6)
            for j in range(4):
                rotate(9 + j, qr[:, j, :], 2)

            def row_max(a):
                ve.wait_ge(sc_done, a + 1)
                link(nc.vector.reduce_max(mx[:, a:a + 1], py[a % 3][:], AX.X))
                ts(nm[:, a:a + 1], mx[:, a:a + 1], -MLA_SCALE, None, ALU.mult).then_inc(nm_ready, 1)

            def row_norm(a):
                ve.wait_ge(exp_done, a + 1)
                link(nc.vector.reciprocal(rrec[:, a:a + 1], rsum[:, a:a + 1]))
                ts(pn[:, a % 2, :], pn[:, a % 2, :], rrec[:, a:a + 1], None, ALU.mult).then_inc(pn_ready, 1)

            def out_low(h):
                ve.wait_ge(oh_ready, h + 1)
                tt(mixl[:, HEADS + h, :], pab[h % 2][:, 0:LAT], mixh[:, HEADS + h, :].bitcast(F32), ALU.subtract).then_inc(ol_ready, 1)

            def out_add(s, b):
                ve.wait_ge(slab_used, MIX0 + S_OUTR + s + 1)
                if s >= 8:
                    ve.wait_ge(y_free, Y_OUT + s - 8 + 1)
                for d in range(2):
                    t = (2 * s + d) % KT
                    ins = stt(xl[:, t, :], b[:, d * LAT:(d + 1) * LAT], ml[:, 5 * KT + t:5 * KT + t + 1], xl[:, t, :], ALU.mult, ALU.add)
                ins.then_inc(y_free, 1)

            row_max(0)
            row_max(1)
            for a in range(16):
                row_norm(a)
                if a + 2 < 16:
                    row_max(a + 2)
                if a % 2 == 1 and a > 1:
                    h = a // 2
                    out_low(h - 1)
                    out_add(h - 1, py[3])
                    static_split(MIX0 + S_OUTR + h + 1)
            out_low(HEADS - 1)
            out_add(HEADS - 1, py[3])
            static_split(MIX0 + S_OUTM + 1)
            for s in range(8):
                out_add(8 + s, py[s % 4])
                if s < 7:
                    static_split(MIX0 + S_OUTM + s + 2)
                for t in (2 * s, 2 * s + 1):
                    square_add(2, t)
            roots(2, 0)
            static_split(FFN2_0 + 1)
            modulate(2, 0, xl, a3l, ml[:, 6 * KT:7 * KT])
            with ve.Fori(0, GROUPS - 1) as i:
                group(i, 1, FFN2_0, LAT, [(xl, g3l, 0)])
            group(GROUPS - 1, 1, FFN2_0, LAT, [(xl, g3l, 0)], None, 3)
            roots(3, 0)
            for t in range(KT):
                stt(xl[:, t, :], xl[:, t, :], vt[:, V_NF + t:V_NF + t + 1], rms[:, 0:LAT], ALU.mult, ALU.mult).then_inc(fin_ready, 1)


_INS = ['x', 'c', 'ctx', 'c_ctx', 'ada_w', 'ada_b', 'norm1_g', 'ffn1_w_in', 'ffn1_w_out', 'norm2_g',
        'mix_w_in', 'ret_decay_fwd', 'ret_decay_bwd', 'mla_q_norm_g', 'mla_w_uq', 'mla_kv_norm_g',
        'mla_w_ukv', 'mix_w_out', 'norm3_g', 'ffn2_w_in', 'ffn2_w_out', 'final_norm_g']


def kernel(**inputs):
    import concourse.bacc as bacc
    from concourse.bass_utils import run_bass_kernel_spmd

    nc = bacc.Bacc("TRN2", target_bir_lowering=False, num_devices=1)
    arrays, args = {}, []
    for name in _INS:
        a = np.ascontiguousarray(inputs[name])
        arrays[f"in_{name}"] = a
        args.append(nc.dram_tensor(f"in_{name}", a.shape, F32, kind="ExternalInput").ap())
    for name, a in constants().items():
        a = np.ascontiguousarray(a)
        arrays[f"in_{name}"] = a
        args.append(nc.dram_tensor(f"in_{name}", a.shape, F32, kind="ExternalInput").ap())
    args.append(nc.dram_tensor("out", (1, LAT, D), F32, kind="ExternalOutput").ap())
    build(nc, *args)
    r = run_bass_kernel_spmd(nc, [arrays], core_ids=[0])
    return r.results[0]["out"]
```
